# Optimizing a Trainium2 kernel written in Bass

```python
import jax, jax.numpy as jnp
from jax import lax
import numpy as np

D_MODEL = 1024
BATCH = 1
SEQ = 256
DEPTH = 2
DEC_BATCH = 8
DEC_SEQ = 4
PAST_LEN = 1024
PAGE_SIZE = 128

N_MIXERS = 2
N_RET_LAYERS = (DEPTH + 1) // 2
N_MOBA_LAYERS = DEPTH // 2
RET_HEADS = 4
RET_DK = 256
RET_DV = 512
RET_CHUNK = 128
RET_QK = RET_HEADS * RET_DK
RET_V = RET_HEADS * RET_DV
MOBA_HEADS = 8
MOBA_DH = 128
MOBA_W = MOBA_HEADS * MOBA_DH
MOBA_BLOCK = 256
MOBA_TOPK = 3
MOBA_QBLK = 16
EPS = 1e-6
NEG = -1e30

kernel_name = "retnet_moba_hybrid_step"

def rmsnorm(x, g):
    xf = x.astype(jnp.float32)
    y = xf * lax.rsqrt(jnp.mean(xf * xf, axis=-1, keepdims=True) + EPS)
    return (y * g.astype(jnp.float32)).astype(x.dtype)

def head_layernorm(x, g):
    xf = x.astype(jnp.float32)
    mu = jnp.mean(xf, axis=-1, keepdims=True)
    xc = xf - mu
    y = xc * lax.rsqrt(jnp.mean(xc * xc, axis=-1, keepdims=True) + EPS)
    return (y * g.astype(jnp.float32)).astype(x.dtype)

def adaln(c, w, b):
    mod = jax.nn.silu(c) @ w + b
    shift, scale, gate = jnp.split(mod, 3, axis=-1)
    return shift[:, None, :], scale[:, None, :], gate[:, None, :]

def ret_log_gamma():
    h = jnp.arange(RET_HEADS, dtype=jnp.float32)
    return jnp.log1p(-jnp.exp2(-5.0 - h))

def alibi_slopes():
    h = jnp.arange(MOBA_HEADS, dtype=jnp.float32)
    return jnp.exp2(-8.0 * (h + 1.0) / MOBA_HEADS)

def retention(q, k, v, s0):
    B, H, T, DK = q.shape
    DV = v.shape[-1]
    C = RET_CHUNK if T % RET_CHUNK == 0 else T
    n = T // C
    log_g = ret_log_gamma()
    i = jnp.arange(C, dtype=jnp.float32)
    diff = i[:, None] - i[None, :]
    decay_mat = jnp.where(diff >= 0, jnp.exp(log_g[:, None, None] * jnp.maximum(diff, 0.0)), 0.0)
    q_decay = jnp.exp(log_g[:, None] * (i + 1.0))[..., None]
    k_decay = jnp.exp(log_g[:, None] * (C - 1.0 - i))[..., None]
    chunk_decay = jnp.exp(log_g * C)[:, None, None]

    def to_chunks(a):
        return a.astype(jnp.float32).reshape(B, H, n, C, a.shape[-1]).transpose(2, 0, 1, 3, 4)

    def step(s, inp):
        qi, ki, vi = inp
        scores = jnp.einsum('bhik,bhjk->bhij', qi, ki) * decay_mat
        inner = jnp.einsum('bhij,bhjv->bhiv', scores, vi)
        cross = jnp.einsum('bhik,bhkv->bhiv', qi * q_decay, s)
        s_new = chunk_decay * s + jnp.einsum('bhjk,bhjv->bhkv', ki * k_decay, vi)
        return s_new, inner + cross

    s_fin, out = lax.scan(step, s0.astype(jnp.float32), (to_chunks(q), to_chunks(k), to_chunks(v)))
    out = out.transpose(1, 2, 0, 3, 4).reshape(B, H, T, DV)
    return out.astype(v.dtype), s_fin

def retention_mixer(h, s0, w_in, gn_g, w_out):
    B, T, _ = h.shape
    proj = h @ w_in
    q, k, v, g = jnp.split(proj, [RET_QK, 2 * RET_QK, 2 * RET_QK + RET_V], axis=-1)
    q = q.reshape(B, T, RET_HEADS, RET_DK).transpose(0, 2, 1, 3)
    k = (k * (RET_DK ** -0.5)).reshape(B, T, RET_HEADS, RET_DK).transpose(0, 2, 1, 3)
    v = v.reshape(B, T, RET_HEADS, RET_DV).transpose(0, 2, 1, 3)
    o, s_fin = retention(q, k, v, s0)
    o = head_layernorm(o.transpose(0, 2, 1, 3), gn_g).reshape(B, T, RET_V)
    return (o * jax.nn.silu(g)) @ w_out, s_fin

def moba_attend(q, k_all, v_all, q_pos):
    B, H, Tq, DH = q.shape
    L = k_all.shape[1]
    nb = L // MOBA_BLOCK
    kb = k_all.reshape(B, nb, MOBA_BLOCK, H, DH)
    vb = v_all.reshape(B, nb, MOBA_BLOCK, H, DH)
    k_mean = jnp.mean(kb.astype(jnp.float32), axis=2)
    topk = min(MOBA_TOPK, nb)
    slopes = alibi_slopes()[None, :, None, None, None]
    qb = MOBA_QBLK if Tq % MOBA_QBLK == 0 else Tq
    nqb = Tq // qb
    q_blocks = q.reshape(B, H, nqb, qb, DH).transpose(2, 0, 1, 3, 4)
    pos_blocks = q_pos.reshape(nqb, qb)
    blk_ids = jnp.arange(nb, dtype=jnp.int32)
    offs = jnp.arange(MOBA_BLOCK, dtype=jnp.int32)
    bi = jnp.arange(B)[:, None, None, None]
    hi = jnp.arange(H)[None, :, None, None]
    scale = DH ** -0.5

    def one(args):
        qi, pi = args
        qf = qi.astype(jnp.float32)
        own = pi // MOBA_BLOCK
        gate_scores = jnp.einsum('bhqd,bnhd->bhqn', qf, k_mean)
        past = blk_ids[None, :] < own[:, None]
        gate_scores = jnp.where(past, gate_scores, NEG)
        _, sel = lax.top_k(gate_scores, topk)
        sel_valid = sel < own[:, None]
        own_b = jnp.broadcast_to(own[:, None], (B, H, qb, 1))
        idx = jnp.concatenate([sel, own_b], axis=-1)
        valid = jnp.concatenate([sel_valid, jnp.ones((B, H, qb, 1), dtype=bool)], axis=-1)
        kg = kb[bi, idx, :, hi].astype(jnp.float32)
        vg = vb[bi, idx, :, hi].astype(jnp.float32)
        kpos = idx[..., None] * MOBA_BLOCK + offs
        dist = pi[:, None, None] - kpos
        s = jnp.einsum('bhqd,bhqnkd->bhqnk', qf, kg) * scale - slopes * dist.astype(jnp.float32)
        s = jnp.where(valid[..., None] & (dist >= 0), s, NEG)
        nsel = idx.shape[-1]
        p = jax.nn.softmax(s.reshape(B, H, qb, nsel * MOBA_BLOCK), axis=-1).reshape(s.shape)
        return jnp.einsum('bhqnk,bhqnkd->bhqd', p, vg)

    out = lax.map(one, (q_blocks, pos_blocks))
    return out.transpose(1, 2, 0, 3, 4).reshape(B, H, Tq, DH)

def moba_mixer(h, k_past, v_past, pos0, w_in, qn_g, kn_g, w_out):
    B, T, _ = h.shape
    proj = h @ w_in
    q, k, v, g = jnp.split(proj, 4, axis=-1)
    q = rmsnorm(q.reshape(B, T, MOBA_HEADS, MOBA_DH), qn_g)
    k = rmsnorm(k.reshape(B, T, MOBA_HEADS, MOBA_DH), kn_g)
    v = v.reshape(B, T, MOBA_HEADS, MOBA_DH)
    past_len = 0 if k_past is None else k_past.shape[1]
    L = past_len + T
    pad = (-L) % MOBA_BLOCK
    zpad = jnp.zeros((B, pad, MOBA_HEADS, MOBA_DH), k.dtype)
    if k_past is None:
        k_all = jnp.concatenate([k, zpad], axis=1)
        v_all = jnp.concatenate([v, zpad], axis=1)
    else:
        k_all = jnp.concatenate([k_past.astype(k.dtype), k, zpad], axis=1)
        v_all = jnp.concatenate([v_past.astype(v.dtype), v, zpad], axis=1)
    q_pos = pos0 + jnp.arange(T, dtype=jnp.int32)
    o = moba_attend(q.transpose(0, 2, 1, 3), k_all, v_all, q_pos)
    o = o.astype(h.dtype).transpose(0, 2, 1, 3).reshape(B, T, MOBA_W)
    return (o * jax.nn.silu(g)) @ w_out, k, v

def setup_inputs(seed: int = 0) -> dict:
    key = jax.random.key(seed)
    ks = jax.random.split(key, 20)
    n_pages = PAST_LEN // PAGE_SIZE
    used = DEC_BATCH * n_pages
    n_pool = used + max(1, used // 4)
    f32 = jnp.float32
    D = D_MODEL
    nrm = lambda k, shape, s: jax.random.normal(k, shape, f32) * s
    page_table = jax.random.permutation(ks[0], n_pool)[:used].reshape(DEC_BATCH, n_pages).astype(jnp.int32)
    return {
        "x_prompt": nrm(ks[1], (BATCH, SEQ, D), 1.0),
        "x_sample": nrm(ks[2], (DEC_BATCH, DEC_SEQ, D), 1.0),
        "c_prompt": nrm(ks[3], (BATCH, D), 1.0),
        "c_sample": nrm(ks[4], (DEC_BATCH, D), 1.0),
        "state_ret": nrm(ks[5], (N_RET_LAYERS, DEC_BATCH, RET_HEADS, RET_DK, RET_DV), 0.1),
        "cache_k": nrm(ks[6], (N_MOBA_LAYERS, n_pool, PAGE_SIZE, MOBA_HEADS, MOBA_DH), 1.0),
        "cache_v": nrm(ks[7], (N_MOBA_LAYERS, n_pool, PAGE_SIZE, MOBA_HEADS, MOBA_DH), 1.0),
        "page_table": page_table,
        "norm_g": 1.0 + nrm(ks[8], (DEPTH, D), 0.02),
        "w_ada": nrm(ks[9], (DEPTH, D, 3 * D), 0.5 * D ** -0.5),
        "b_ada": nrm(ks[10], (DEPTH, 3 * D), 0.02),
        "w_ret_in": nrm(ks[11], (N_RET_LAYERS, D, 2 * RET_QK + 2 * RET_V), D ** -0.5),
        "ret_gn_g": 1.0 + nrm(ks[12], (N_RET_LAYERS, RET_HEADS, RET_DV), 0.02),
        "w_ret_out": nrm(ks[13], (N_RET_LAYERS, RET_V, D), RET_V ** -0.5),
        "w_moba_in": nrm(ks[14], (N_MOBA_LAYERS, D, 4 * MOBA_W), D ** -0.5),
        "moba_q_g": 1.0 + nrm(ks[15], (N_MOBA_LAYERS, MOBA_DH), 0.02),
        "moba_k_g": 1.0 + nrm(ks[16], (N_MOBA_LAYERS, MOBA_DH), 0.02),
        "w_moba_out": nrm(ks[17], (N_MOBA_LAYERS, MOBA_W, D), MOBA_W ** -0.5),
    }

def reference(x_prompt, x_sample, c_prompt, c_sample, state_ret, cache_k, cache_v, page_table,
              norm_g, w_ada, b_ada, w_ret_in, ret_gn_g, w_ret_out,
              w_moba_in, moba_q_g, moba_k_g, w_moba_out):
    yp, ys = x_prompt, x_sample
    Bp = x_prompt.shape[0]
    Bs, Ts, _ = x_sample.shape
    ret_p, ret_s, kp_l, vp_l, ks_l, vs_l = [], [], [], [], [], []
    for layer in range(DEPTH):
        j = layer // N_MIXERS
        sh_p, sc_p, gt_p = adaln(c_prompt, w_ada[layer], b_ada[layer])
        sh_s, sc_s, gt_s = adaln(c_sample, w_ada[layer], b_ada[layer])
        hp = rmsnorm(yp, norm_g[layer]) * (1.0 + sc_p) + sh_p
        hs = rmsnorm(ys, norm_g[layer]) * (1.0 + sc_s) + sh_s
        if layer % N_MIXERS == 0:
            s0 = jnp.zeros((Bp, RET_HEADS, RET_DK, RET_DV), jnp.float32)
            op, sp = retention_mixer(hp, s0, w_ret_in[j], ret_gn_g[j], w_ret_out[j])
            os_, ss = retention_mixer(hs, state_ret[j], w_ret_in[j], ret_gn_g[j], w_ret_out[j])
            ret_p.append(sp.astype(x_prompt.dtype))
            ret_s.append(ss.astype(x_sample.dtype))
        else:
            past_len = page_table.shape[1] * PAGE_SIZE
            k_past = cache_k[j][page_table].reshape(Bs, past_len, MOBA_HEADS, MOBA_DH)
            v_past = cache_v[j][page_table].reshape(Bs, past_len, MOBA_HEADS, MOBA_DH)
            op, kpn, vpn = moba_mixer(hp, None, None, 0, w_moba_in[j], moba_q_g[j], moba_k_g[j], w_moba_out[j])
            os_, ksn, vsn = moba_mixer(hs, k_past, v_past, past_len, w_moba_in[j], moba_q_g[j], moba_k_g[j], w_moba_out[j])
            kp_l.append(kpn)
            vp_l.append(vpn)
            ks_l.append(ksn)
            vs_l.append(vsn)
        yp = yp + gt_p * op
        ys = ys + gt_s * os_
    return (yp, ys, jnp.stack(ret_p), jnp.stack(ret_s), jnp.stack(kp_l), jnp.stack(vp_l), jnp.stack(ks_l), jnp.stack(vs_l))


_drawn_inputs = setup_inputs


def setup_inputs(seed=0):
    import zlib

    import numpy as np

    out = dict(_drawn_inputs(seed))
    spreads = {}
    factors = {}
    for name, (base, spread) in spreads.items():
        noise = np.random.default_rng([zlib.crc32(name.encode()), seed]).standard_normal(out[name].shape)
        drawn = base * np.exp(spread * noise) if base else spread * noise
        out[name] = __import__('jax').numpy.asarray(drawn.astype(out[name].dtype))
    for name, factor in factors.items():
        out[name] = (out[name] * factor).astype(out[name].dtype)
    return out
```

```python
from contextlib import ExitStack

import numpy as np

import concourse.bass as bass
from concourse import mybir

F32 = mybir.dt.float32
F32R = mybir.dt.float32r
I32 = mybir.dt.int32
ALU = mybir.AluOpType
ACT = mybir.ActivationFunctionType
AX_X = mybir.AxisListType.X

P = 128
D = 1024
KT = D // P
CH = 512
NP = 256
NS = 8
TS = 4
ROWS = NP + NS * TS
RH, DK, DV = 4, 256, 512
MH, DH = 8, 128
PAGES = 8
PAST = PAGES * P
EPS = 1e-6
NEG = -1e30
RING = 4
ADA_FIRST, ADA_GATE = (2, 3, 0, 1), (4, 5)
RET_VT = RH * DV // P

CONSTS_FIRST = [("ident", P), ("rep", P), ("pick_prompt", P), ("pick_seq", P), ("eps", 1)]
CONSTS = CONSTS_FIRST + [
    ("pick_den", P), ("dec_p", RH * P), ("dec_s", RH * 32), ("qdec_p", RH), ("kdec_p", RH), ("qdec_s", RH),
    ("kdec_s", RH), ("kmask_s", NS), ("tie", 4), ("hmask", 2), ("dist_p", 3 * P), ("alibi", 2 * P),
    ("alibi_new", NS * 32)]


def const_columns():
    at, out = 0, {}
    for name, n in CONSTS:
        out[name] = (at, n)
        at += n
    return out, at


def const_table():
    where, width = const_columns()
    t = np.zeros((P, width), np.float64)
    p = np.arange(P)

    def put(name, a):
        at, n = where[name]
        t[:, at:at + n] = np.asarray(a, np.float64).reshape(P, n)

    put("ident", np.eye(P))
    put("rep", (p[:, None] % 32) == (p[None, :] % 32))
    put("pick_prompt", np.repeat((p % 32 == 0)[:, None], P, 1))
    put("pick_seq", (p[:, None] % 32) == 1 + (p[None, :] % 32) // TS)
    put("pick_den", (p[:, None] // 32 == p[None, :] // 32) & (p[:, None] % 4 == p[None, :] % 4)
        & ((p[:, None] % 8) // 4 == (p[None, :] % 8) // 4))
    gamma = 1.0 - 2.0 ** (-5.0 - np.arange(RH))
    i = np.arange(P)
    put("dec_p", (gamma[None, :, None] ** -(i[:, None, None] + 1.0)) * (i[None, None, :] >= i[:, None, None]))
    r = np.arange(32)
    same = (p[:, None] < 32) & (p[:, None] // TS == r[None, :] // TS) & (r[None, :] % TS >= p[:, None] % TS)
    put("dec_s", (gamma[None, :, None] ** -(p[:, None, None] % TS + 1.0)) * same[:, None, :])
    put("qdec_p", gamma[None, :] ** (i[:, None] + 1.0))
    put("kdec_p", gamma[None, :] ** (P - 1.0 - i[:, None]) * DK ** -0.5)
    put("qdec_s", gamma[None, :] ** (p[:, None] % TS + 1.0))
    put("kdec_s", gamma[None, :] ** (TS - 1.0 - p[:, None] % TS) * DK ** -0.5)
    put("kmask_s", (p[:, None] % 32) // TS == np.arange(NS)[None, :])
    put("tie", np.repeat(np.array([[1, 2, 3, 4]]), P, 0))
    put("hmask", ((p[:, None] % 32) < 8) & ((p[:, None] % 32) // 4 == np.arange(2)[None, :]))
    put("eps", np.full((P, 1), EPS))
    dist = np.full((P, 3 * P), 1e33)
    d0 = p[:, None] - p[None, :]
    dist[:, 0:P] = np.where(d0 >= 0, d0, 1e33)
    d1 = P + p[:, None] - np.arange(2 * P)[None, :]
    dist[:, P:3 * P] = np.where(d1 >= 0, d1, 1e33)
    put("dist_p", dist)
    g, ii, h2, q = p // 32, (p % 32) // 8, (p % 8) // 4, p % 4
    slope = 2.0 ** (-8.0 * (2 * g + h2 + 1.0) / MH)
    kpos = (np.arange(PAGES)[:, None] * P + np.arange(32)[None, :]).reshape(-1)
    put("alibi", -slope[:, None] * (PAST + q[:, None] - kpos[None, :] - 32 * ii[:, None]))
    s, key = np.arange(NS), np.arange(32)
    ok = ((ii[:, None, None] == 0) & (key[None, None, :] // TS == s[None, :, None])
          & (key[None, None, :] % TS <= q[:, None, None]))
    put("alibi_new", np.where(ok, -slope[:, None, None] * (q[:, None, None] - key[None, None, :] % TS), NEG))
    return t.astype(np.float32)


ADA_AT = {RH - 1: [(0, c) for c in ADA_GATE]}
G_AFTER = 3
SPLIT = [("ret", h, b) for h in range(RH) for b in range(3)] + [("moba", c, 0) for c in range(6)]
LOW_BY = {u: "vector" if u[0] == "ret" and u[2] else "gpsimd" for u in SPLIT}
LOW_LAG = 2


def stream_units():
    units = [("ada", 0, c) for c in ADA_FIRST]
    for h in range(RH):
        units += [("ret", h, 0), ("ret", h, 1), ("ret", h, 2)]
        units += [("ada",) + x for x in ADA_AT.get(h, ())]
        units += [("state", h, 0), ("state", h, 1)]
    units += [("rout", 0, 0), ("rout", 0, 1)] + [("ada", 1, c) for c in ADA_FIRST[:3]]
    units += [("rout", 1, 0), ("rout", 1, 1)]
    units += [("ada", 1, c) for c in ADA_FIRST[3:] + ADA_GATE]
    units += [("moba", c, 0) for c in range(6)]
    for s in range(NS):
        units += [("k", s, 0), ("k", s, 1)]
        if s == NS - 1:
            units.append(("mout", 0, 0))
        if s == 0:
            units.append(("moba", 6, 0))
        if s == 1:
            units.append(("v", 0, 1))
        units.append(("v", s, 0))
        if s:
            units.append(("v", s, 1))
        if s == G_AFTER:
            units.append(("moba", 7, 0))
    return units


def bank_plan():
    plan, count, turn = {}, [0] * 8, {"pair": 0, "misc": 0}

    def use(label, bank):
        plan[label] = (bank, count[bank])
        count[bank] += 1

    def misc(label):
        use(label, 6 + turn["misc"] % 2)
        turn["misc"] += 1

    def pair(a, b):
        k = 2 * (turn["pair"] % 2)
        turn["pair"] += 1
        use(a, k)
        use(b, k + 1)

    def project(tag):
        use(("part",) + tag, 4)
        pair(("row",) + tag + (0,), ("row",) + tag + (1,))
        use(("row",) + tag + (2,), 5)

    def ada(layer, chunks):
        for c in chunks:
            use(("part", "ada", layer, c), 4)
            pair(("mod", layer, c, 0), ("mod", layer, c, 1))

    def turn_h(layer):
        for n in range(3):
            misc(("hT", layer, n, 0))
            misc(("hT", layer, n, 1))

    misc(("cT", 0))
    misc(("cT", 1))
    ada(0, ADA_FIRST)
    turn_h(0)

    def new(h, s):
        misc(("new", h, s, 0))
        misc(("new", h, s, 1))

    for h in range(RH):
        use(("part", "ret", h, 0), 4)
        pair(("row", "ret", h, 0, 0), ("row", "ret", h, 0, 1))
        for s in range(NS if h else 0):
            new(h - 1, s)
        use(("row", "ret", h, 0, 2), 5)
        project(("ret", h, 1))
        if h:
            for n in range(3):
                misc(("yT", h - 1, n))
        for n in range(3):
            misc(("qkT", h, n))
        project(("ret", h, 2))
        for layer, c in ADA_AT.get(h, ()):
            ada(layer, (c,))
        misc(("scores", h))
        misc(("S1", h, 0))
        misc(("S1", h, 1))
        use(("part", "o", h), 4)
        pair(("row", "o", h, 0), ("row", "o", h, 1))
        use(("row", "o", h, 2), 5)
        misc(("S2", h, 0))
        misc(("S2", h, 1))
    for s in range(NS):
        new(RH - 1, s)
    for n in range(3):
        misc(("yT", RH - 1, n))
    project(("rout", 0))
    ada(1, ADA_FIRST[:3])
    project(("rout", 1))
    ada(1, ADA_FIRST[3:] + ADA_GATE)
    turn_h(1)

    def turn_rows(which):
        for n in range(2):
            misc(("pT", which, n, 0))
            misc(("pT", which, n, 1))

    for c in range(6):
        use(("part", "moba", c), 4)
        pair(("row", "moba", c, 0), ("row", "moba", c, 1))
        if c >= 4:
            turn_rows(c - 4)
        use(("row", "moba", c, 2), 5)

    def prompt_values(h):
        use(("pP", h), 1)
        use(("pO", h), 2)

    def g_chunk(c, tiles):
        for n in tiles:
            if n == 0:
                use(("part", "moba", c), 4)
            use(("row", "moba", c, n), 3 * n)
            if n == 1:
                use(("row", "moba", c, 2), 5)

    use(("pS", 0), 0)
    g_chunk(6, (0,))
    prompt_values(0)
    for s in range(NS):
        if s + 1 < MH:
            use(("pS", s + 1), 0)
        if s == NS - 1:
            use(("pY", s - 1), 3)
            use(("pY", s), 3)
            pair(("row", "mout", 0, 0), ("row", "mout", 0, 1))
        use(("QK", s), 6)
        if s == 0:
            g_chunk(6, (1,))
        if s:
            use(("OT", s - 1), 5)
        if s + 1 < MH:
            prompt_values(s + 1)
        if 0 < s < NS - 1:
            use(("pY", s - 1), 3)
        use(("PT", s), 4)
        use(("PV", s), 7)
        if s == G_AFTER:
            g_chunk(7, range(2))
            use(("GT", 0), 4)
            use(("GT", 1), 5)
    pair(("row", "mout", 1, 0), ("row", "mout", 1, 1))
    use(("OT", NS - 1), 5)
    for c in range(2):
        use(("part", "mout", c), 4)
        use(("row", "mout", c, 2), 5)
    return plan


def build(nc, t):
    units = stream_units()
    unit_at = {u: n for n, u in enumerate(units)}
    plan = bank_plan()
    cols, cwidth = const_columns()
    landed_at, total = [], [0] * RING
    for n, (kind, a, b) in enumerate(units):
        pieces = 4 if kind in ("state", "k", "v") else 2 if kind == "ret" and b == 0 else 1
        total[n % RING] += 16 * pieces
        landed_at.append(total[n % RING])

    with ExitStack() as ctx:
        def sem(name):
            return ctx.enter_context(nc.semaphore(name))

        def sb(name, shape, dt=F32):
            return ctx.enter_context(nc.sbuf_tensor(name, shape, dt))

        ring_at = -(-nc.sbuf_base // 32) * 32
        ring = sb("ring", [P, RING, KT * CH])
        consts = sb("consts", [P, cwidth])
        X = sb("x_rows", [P, 3, D])
        mod_at = -(-nc.sbuf_base // 32) * 32
        mod = sb("modulation", [P, 3, 2, D])
        hT_at = -(-nc.sbuf_base // 32) * 32
        hT = sb("h_turned", [P, KT, ROWS])
        norm_b = sb("norm_gain", [P, D])
        bias_ada = sb("ada_bias", [P, CH])
        cT = sb("c_turned", [P, KT, 32])
        part = sb("partial", [P, CH])
        stat = sb("stats", [P, 96])
        ptab = sb("pages", [1, NS * PAGES], I32)

        spec0 = [("y", (3, DV)), ("G", (3, DV)), ("q", (3, DK)), ("k", (3, DK)), ("kd", (2, DK)),
                 ("kM", (NS, DK)), ("kx", (DK,)), ("kmix", (DK,)), ("vmix", (DV,)), ("v", (3, DV)),
                 ("qkT", (3, 4, P)), ("qpad", (2, NS * (32 + TS))),
                 ("sT", (2, P)), ("sTs", (32,)), ("S1", (2, DV)), ("yT", (RET_VT, ROWS)), ("gn", (RH * DV,))]
        spec1 = [("qbT", (MH * 4, 32)), ("qd", (2, D)), ("v", (3, D)),
                 ("kt", (MH * 4, 2 * P + 32)), ("G", (3, D)), ("x", (288,)), ("PTs", (3, P)),
                 ("px", (3 * P,)), ("pPT", (3, P)), ("oc", (P,)), ("py", (2, DH))]
        size = max(sum(int(np.prod(shape)) for _, shape in spec) for spec in (spec0, spec1))
        arena_at = -(-nc.sbuf_base // 32) * 32
        arena = sb("arena", [P, size])

        def place(spec):
            at, out = 0, {}
            for name, shape in spec:
                n = int(np.prod(shape))
                v = arena[:, at:at + n]
                if len(shape) == 2:
                    v = v.rearrange("p (a b) -> p a b", a=shape[0])
                if len(shape) == 3:
                    v = v.rearrange("p (a b c) -> p a b c", a=shape[0], b=shape[1])
                out[name] = v
                at += n
            return out, at

        def rounded(name, shape, at):
            return nc.alloc_sbuf_tensor_at(name, [P] + list(shape), F32R, offset=at)

        def in_arena(spec, name):
            return arena_at + 4 * sum(int(np.prod(sh)) for _, sh in spec[:[x for x, _ in spec].index(name)])

        L0, _ = place(spec0)
        kM = rounded("keys_by_sequence", (NS, DK), in_arena(spec0, "kM"))
        kmix = rounded("key_parts", (DK,), in_arena(spec0, "kmix"))
        vmix = rounded("value_parts", (DV,), in_arena(spec0, "vmix"))
        h_high = rounded("h_high", (KT, ROWS), hT_at)
        w_low = rounded("weights_low", (RING, KT, CH), ring_at)
        w_high = [rounded("weights_high_0", (KT, CH), mod_at),
                  rounded("weights_high_1", (KT, CH), in_arena(spec1, "G") - 4 * 3 * D)]
        h_low = [rounded("h_low_0", (KT, NP), mod_at + 4 * 4 * D),
                 rounded("h_low_1", (KT, NP), in_arena(spec1, "G") + 4 * D)]
        L1, end1 = place(spec1)
        h_rows = arena[:, 0:3 * D].rearrange("p (a b) -> p a b", a=3)
        c_rows = L0["kM"].rearrange("p a b -> p (a b)")[:, 0:D]
        row_qk = L1["kt"].rearrange("p a b -> p (a b)")[:, 0:6 * D].rearrange(
            "p (w n c) -> p w n c", w=2, n=3)
        squares = arena[:, end1 - 9 * P:end1 - 9 * P + CH]
        gains = arena[:, end1 - 2 * DH:end1].rearrange("p (a b) -> p a b", a=2)
        GT = norm_b[:, 0:MH * 32].rearrange("p (a b) -> p a b", a=MH)
        oT = norm_b[:, 256:512].rearrange("p (a b) -> p a b", a=MH)
        py = [L1["py"], norm_b[:, 512:768].rearrange("p (a b) -> p a b", a=2)]
        kbT = norm_b[:, :].rearrange("p (a b) -> p a b", b=32)
        soft = cT[:, :, :].rearrange("p a b -> p (a b)")
        pqT = mod[:, 0, :, :].rearrange("p a b -> p (a b)").rearrange("p (h t) -> p h t", h=MH)
        pkT = mod[:, 1, :, :].rearrange("p a b -> p (a b)").rearrange("p (h t) -> p h t", h=MH)
        w_last = L1["kt"].rearrange("p a b -> p (a b)")[:, 0:KT * CH].rearrange(
            "p (k n) -> p k n", k=KT)
        pyT = pqT
        bank = [ctx.enter_context(nc.psum_tensor(f"bank{b}", [P, CH], F32)) for b in range(8)]

        def const(name, pattern=None, **kw):
            at, n = cols[name]
            v = consts[:, at:at + n]
            return v.rearrange(pattern, **kw) if pattern else v

        ident = const("ident")
        SUMSQ, ROOT, RSTD, MEANVAR, SD, RSD = 0, 3, 6, 10, 16, 19
        MS, MSD, RMS4, BN = 24, 28, 32, 36
        PNEG, PSUM, PRS = 42, 44, 46
        DEN, RDEN, PICK, LOW, TOPT, TIE = 48, 49, 50, 52, 53, 54
        PEN, BMAX, MAXB, BIAS, SUMS, DENS = 58, 62, 66, 68, 74, 80

        def st(at, n=1):
            return stat[:, at:at + n]

        landed = [sem(f"landed{i}") for i in range(RING)]
        full = [sem(f"bank_full{b}") for b in range(8)]
        free = [sem(f"bank_read{b}") for b in range(8)]
        half_used = sem("half_used")
        consts_in, x_in, c_in, gn_in, gains_in, pages_in = (
            sem(n) for n in ("consts_in", "x_in", "c_in", "gn_in", "gains_in", "pages_in"))
        bias_in, tables_in = sem("bias_in"), sem("tables_in")
        norm_in = [sem(f"norm_in{i}") for i in range(2)]
        k_parts, v_parts = sem("k_parts"), sem("v_parts")
        psum_zeroed, pool_zeroed, c_silu = sem("psum_zeroed"), sem("pool_zeroed"), sem("c_silu")
        sumsq, root, dve_step, h_ready = sem("sumsq"), sem("root"), sem("dve_step"), sem("h_ready")
        kM_ready, gate_ready, sT_ready = (sem(n) for n in ("kM_ready", "gate_ready", "sT_ready"))
        state_new = sem("state_new")
        state_out = [sem(f"state_out{i}") for i in range(2 * RH)]
        var_ready, sd_ready, y_ready, x_done = (sem(n) for n in ("var_ready", "sd_ready", "y_ready", "x_done"))
        sq_ready, ms_ready, msd_ready, qk_rows = (sem(n) for n in ("sq_ready", "ms_ready", "msd_ready", "qk_rows"))
        yTs_ready = sem("yTs_ready")
        h_high_ready, high_ready, high_used = sem("h_high_ready"), sem("high_ready"), sem("high_used")
        low_ready = {e: sem("low_ready_" + e) for e in ("vector", "gpsimd")}
        h_joined = sem("h_joined")
        w_last_in, y_out = sem("w_last_in"), sem("y_out")
        v_half_used = sem("v_half_used")
        qb_ready, qd_ready, kt_ready, new_k_ready = (
            sem(n) for n in ("qb_ready", "qd_ready", "kt_ready", "new_k_ready"))
        bias_ready, P_ready, px_ready, pP_ready, pr_ready, py_ready = (
            sem(n) for n in ("bias_ready", "P_ready", "px_ready", "pP_ready", "pr_ready", "py_ready"))
        prompt_state_out, k_out, rows_out = sem("prompt_state_out"), sem("k_out"), sem("rows_out")

        def wait_full(eng, label):
            b, n = plan[label]
            eng.wait_ge(full[b], n + 1)
            return bank[b]

        def wait_read(eng, label):
            b, n = plan[label]
            eng.wait_ge(free[b], n + 1)

        def wait_unit(eng, u):
            n = unit_at[u]
            eng.wait_ge(landed[n % RING], landed_at[n])
            return ring[:, n % RING, :]

        def sealed(ins, label):
            ins.then_inc(full[plan[label][0]], 1)

        def read_out(ins, label):
            ins.then_inc(free[plan[label][0]], 1)

        def state_slot(h, s):
            return ring[:, unit_at[("state", h, s // 4)] % RING, :].rearrange(
                "p (s k v) -> p s k v", s=4, k=2)[:, s % 4, :, :]

        def split_at(u):
            n = SPLIT.index(u)
            return n, sum(LOW_BY[x] == LOW_BY[u] for x in SPLIT[:n])

        def low_weights(eng, tensor_tensor, u):
            n, m = split_at(u)
            tag = u if u[0] == "ret" else u[:2]
            high = w_high[u[0] == "moba"]
            wait_full(eng, ("part",) + tag)
            slot = unit_at[u] % RING
            for k in range(KT):
                eng.wait_ge(high_ready, 4 * n + k // 2 + 1)
                tensor_tensor(w_low[:, slot, k, :], ring[:, slot, k * CH:(k + 1) * CH], high[:, k, :].bitcast(F32),
                              ALU.subtract).then_inc(low_ready[LOW_BY[u]], 1)

        block = ctx.enter_context(nc.Block())

        @block.sync
        def _(sp):
            def released(n):
                kind, a, b = units[n]
                if kind == "ada":
                    wait_full(sp, ("part", "ada", a, b))
                elif kind == "ret":
                    wait_full(sp, ("row", "ret", a, b, 1))
                elif kind == "rout" and b == 0:
                    sp.wait_ge(half_used, a + 1)
                elif kind in ("rout", "moba"):
                    wait_full(sp, ("row", kind, a, 1))
                elif kind == "state":
                    for s in range(4 * b, 4 * b + 4):
                        sp.wait_ge(state_new, NS * a + s + 1)
                        sp.dma_start(t["state_sample"][0, s, a].rearrange("(k p) v -> p k v", p=P),
                                     state_slot(a, s)).then_inc(state_out[2 * a + b], 16)
                    sp.wait_ge(state_out[2 * a + b], 64)
                elif kind == "k":
                    sp.wait_ge(kt_ready, 8 * a + 4 * b + 4)
                elif kind == "v" and b == 0:
                    sp.wait_ge(v_half_used, a + 1)
                elif kind == "v":
                    wait_full(sp, ("PV", a))

            xs = t["x_sample"].rearrange("b s d -> (b s) d")
            first = sum(n for _, n in CONSTS_FIRST)
            sp.dma_start(consts[:, 0:first], t["consts"][:, 0:first]).then_inc(consts_in, 16)
            page = {}
            for n, (kind, a, b) in enumerate(units):
                if n == 1:
                    sp.wait_ge(pool_zeroed, 2)
                    sp.dma_start(c_rows[0:1, :], t["c_prompt"]).then_inc(c_in, 16)
                    sp.dma_start(c_rows[1:1 + NS, :], t["c_sample"]).then_inc(c_in, 16)
                    sp.dma_start(bias_ada[0:12, :], t["b_ada"].rearrange("l (c n) -> (l c) n", c=6)).then_inc(bias_in, 16)
                    sp.dma_start(norm_b[:, :], t["norm_g"][0:1, :].partition_broadcast(P)).then_inc(norm_in[0], 16)
                if n == len(ADA_FIRST):
                    sp.dma_start(consts[:, first:], t["consts"][:, first:]).then_inc(tables_in, 16)
                if n == 3:
                    sp.dma_start(X[:, 0:2, :], t["x_prompt"][0].rearrange("(n p) d -> p n d", p=P)).then_inc(x_in, 16)
                    for i in range(4):
                        sp.dma_start(X[32 * i:32 * i + 32, 2, :], xs).then_inc(x_in, 16)
                if n >= RING:
                    released(n - RING)
                slot, got = ring[:, n % RING, :], landed[n % RING]
                w = slot.rearrange("p (k n) -> p k n", k=KT)
                if kind == "ada":
                    src = t["w_ada"][a].rearrange("(k p) n -> p k n", p=P)
                    sp.dma_start(w, src[:, :, b * CH:(b + 1) * CH]).then_inc(got, 16)
                elif kind == "ret":
                    src = t["w_ret_in"][0].rearrange("(k p) n -> p k n", p=P)
                    if b == 0:
                        sp.dma_start(w[:, :, 0:DK], src[:, :, a * DK:(a + 1) * DK]).then_inc(got, 16)
                        at = RH * DK + a * DK
                        sp.dma_start(w[:, :, DK:2 * DK], src[:, :, at:at + DK]).then_inc(got, 16)
                    else:
                        at = 2 * RH * DK + (b - 1) * RH * DV + a * DV
                        sp.dma_start(w, src[:, :, at:at + DV]).then_inc(got, 16)
                elif kind == "state":
                    for s in range(4 * b, 4 * b + 4):
                        sp.dma_start(state_slot(a, s), t["state_ret"][0, s, a].rearrange("(k p) v -> p k v", p=P)
                                     ).then_inc(got, 16)
                elif kind == "rout":
                    src = t["w_ret_out"][0, b * D:(b + 1) * D].rearrange("(k p) n -> p k n", p=P)
                    sp.dma_start(w, src[:, :, a * CH:(a + 1) * CH]).then_inc(got, 16)
                elif kind in ("moba", "mout"):
                    src = t["w_moba_in" if kind == "moba" else "w_moba_out"][0].rearrange("(k p) n -> p k n", p=P)
                    sp.dma_start(w, src[:, :, a * CH:(a + 1) * CH]).then_inc(got, 16)
                elif kind == "k":
                    if a == 0 and b == 0:
                        sp.dma_start(ptab[:, :], t["page_table"].rearrange("(o b) n -> o (b n)", o=1)
                                     ).then_inc(pages_in, 16)
                        sp.wait_ge(pages_in, 16)
                    if b == 0:
                        page[a] = [sp.value_load(ptab[0:1, PAGES * a + j:PAGES * a + j + 1], min_val=0,
                                                 max_val=t["cache_k"].shape[1] - 1) for j in range(PAGES)]
                    for j in range(4):
                        src = t["cache_k"][0, bass.ds(page[a][4 * b + j], 1)].rearrange("o p h d -> (o p) (h d)")
                        sp.dma_start(slot[:, j * D:(j + 1) * D], src).then_inc(got, 16)
                elif kind == "v":
                    for j in range(4):
                        src = t["cache_v"][0, bass.ds(page[a][4 * b + j], 1)].rearrange(
                            "o (i p) h d -> (o p) i (h d)", p=32)
                        sp.dma_start(slot[32 * j:32 * j + 32, :].rearrange("p (i n) -> p i n", i=4),
                                     src).then_inc(got, 16)
            wait_full(sp, ("QK", NS - 1))
            sp.dma_start(w_last, t["w_moba_out"][0].rearrange("(k p) n -> p k n", p=P)[:, :, CH:2 * CH]
                         ).then_inc(w_last_in, 16)
            yp = t["y_prompt"][0].rearrange("(n p) d -> n p d", p=P)
            ys = t["y_sample"].rearrange("b s d -> (b s) d")
            for n in range(3):
                sp.wait_ge(x_done, 3 + n + 1)
                sp.dma_start(yp[n] if n < 2 else ys, X[:, n, :] if n < 2 else X[0:32, 2, :]).then_inc(y_out, 16)
            sp.wait_ge(y_out, 48)

        @block.tensor
        def _(pe):
            opened = [0] * 8

            def open_bank(label):
                b, n = plan[label]
                assert opened[b] == n, label
                opened[b] += 1
                if n:
                    pe.wait_ge(free[b], n)
                return bank[b]

            def add_groups(tag):
                label = ("row",) + tag + (2,)
                o = open_bank(label)
                wait_read(pe, ("part",) + tag)
                sealed(pe.matmul(o[:, :], const("rep"), part[:, :], start=True, stop=True), label)

            def project(tag, xT, tiles, between=None, before_half=None):
                outs, halves = {}, len(tiles)
                for half in range(halves):
                    if half and before_half:
                        before_half()
                    w = wait_unit(pe, tiles[half]).rearrange("p (k n) -> p k n", k=KT)
                    ends = half == halves - 1
                    for n in (2, 0, 1):
                        label = ("part",) + tag if n == 2 else ("row",) + tag + (n,)
                        if half == 0:
                            outs[n] = open_bank(label)
                        o = outs[n]
                        for k in range(KT):
                            kk = half * KT + k
                            if n == 2:
                                g = 32 * (k % 4)
                                last = pe.matmul(o[g:g + 32, :], xT[:, kk, NP:ROWS], w[:, k, :],
                                                 start=kk < 4, stop=ends and k >= 4)
                            else:
                                if between and half == 0:
                                    between(KT * n + k)
                                last = pe.matmul(o[:, :], xT[:, kk, n * P:(n + 1) * P], w[:, k, :],
                                                 start=kk == 0, stop=ends and k == KT - 1)
                        if ends:
                            sealed(last, label)
                        elif n == 1:
                            last.then_inc(half_used, 1)
                add_groups(tag)

            def project_parts(tag, unit, between=None):
                n, m = split_at(unit)
                layer = int(unit[0] == "moba")
                xs = [[part_[:, :, i * P:(i + 1) * P] for i in range(2)] for part_ in (h_high, h_low[layer])]
                high, low = w_high[layer], w_low[:, unit_at[unit] % RING]
                w = wait_unit(pe, unit).rearrange("p (k n) -> p k n", k=KT)
                o = open_bank(("part",) + tag)
                for k in range(KT):
                    g = 32 * (k % 4)
                    last = pe.matmul(o[g:g + 32, :], hT[:, k, NP:ROWS], w[:, k, :], start=k < 4, stop=k >= 4)
                sealed(last, ("part",) + tag)
                o = [open_bank(("row",) + tag + (i,)) for i in range(2)]
                for k in range(KT + LOW_LAG):
                    if k < KT:
                        if k % 2 == 0:
                            pe.wait_ge(high_ready, 4 * n + k // 2 + 1)
                        for i in range(2):
                            for p in range(2):
                                pe.matmul(o[i][:, :], xs[p][i][:, k, :], high[:, k, :],
                                          start=k == 0 and p == 0, stop=False)
                    if between:
                        between(k)
                    if k >= LOW_LAG:
                        kk = k - LOW_LAG
                        pe.wait_ge(low_ready[LOW_BY[unit]], KT * m + kk + 1)
                        for i in range(2):
                            last = pe.matmul(o[i][:, :], xs[0][i][:, kk, :], low[:, kk, :], start=False,
                                             stop=kk == KT - 1)
                            if kk == KT - 1:
                                sealed(last, ("row",) + tag + (i,))
                            elif i == 1 and kk % 2:
                                last.then_inc(high_used, 1)
                add_groups(tag)

            def ada(layer, chunks):
                for c in chunks:
                    label = ("part", "ada", layer, c)
                    w = wait_unit(pe, ("ada", layer, c)).rearrange("p (k n) -> p k n", k=KT)
                    o = open_bank(label)
                    one = 6 * layer + c
                    pe.matmul(o[0:32, :], ident[:, one:one + 1].broadcast_to([P, 32]), bias_ada[:, :],
                              start=True, stop=False)
                    for k in range(KT):
                        g = 32 * (k % 4)
                        last = pe.matmul(o[g:g + 32, :], cT[:, k, :], w[:, k, :], start=0 < k < 4, stop=k >= 4)
                    sealed(last, label)
                    for n, pick in ((0, "pick_prompt"), (1, "pick_seq")):
                        o = open_bank(("mod", layer, c, n))
                        wait_read(pe, label)
                        sealed(pe.matmul(o[:, :], const(pick), part[:, :], start=True, stop=True),
                               ("mod", layer, c, n))

            def turn(label, srcs):
                o = open_bank(label)
                for i, src in enumerate(srcs):
                    last = pe.transpose(o[:, i * P:(i + 1) * P], src, ident)
                sealed(last, label)

            def turn_h(layer):
                for n in range(3):
                    pe.wait_ge(h_ready, 3 * layer + n + 1)
                    for half in range(2):
                        turn(("hT", layer, n, half),
                             [h_rows[:, n, (4 * half + k) * P:(4 * half + k + 1) * P] for k in range(4)])
                for n in range(3):
                    for half in range(2):
                        wait_read(pe, ("hT", layer, n, half))

            def turn_y(h):
                for n in range(3):
                    pe.wait_ge(y_ready, 3 * h + n + 1)
                    turn(("yT", h, n), [L0["y"][:, n, k * P:(k + 1) * P] for k in range(4)])

            pe.wait_ge(consts_in, 16)
            pe.wait_ge(psum_zeroed, 1)
            pe.wait_ge(c_silu, 1)
            for half in range(2):
                turn(("cT", half), [c_rows[:, (4 * half + k) * P:(4 * half + k + 1) * P] for k in range(4)])
            for half in range(2):
                wait_read(pe, ("cT", half))
            pe.wait_ge(bias_in, 16)
            ada(0, ADA_FIRST)
            turn_h(0)

            q, k, kd, v, qkT = (L0[x] for x in ("q", "k", "kd", "v", "qkT"))

            def new(h, s, j):
                if s == 0 and j == 0:
                    pe.wait_ge(kM_ready, h + 1)
                    pe.wait_ge(v_parts, 2 * h + 2)
                o = open_bank(("new", h, s, j))
                sealed(pe.matmul(o[:, :], kM[:, s, j * P:(j + 1) * P], vmix[:, :], start=True, stop=True),
                       ("new", h, s, j))

            def new_of_head_before(k):
                if k < NS:
                    for j in range(2):
                        new(h - 1, k, j)

            for h in range(RH):
                project_parts(("ret", h, 0), ("ret", h, 0), new_of_head_before if h else None)
                project_parts(("ret", h, 1), ("ret", h, 1))
                if h:
                    turn_y(h - 1)
                for n in range(3):
                    wait_read(pe, ("row", "ret", h, 0, n))
                    turn(("qkT", h, n), [q[:, n, 0:P], q[:, n, P:DK], k[:, n, 0:P], k[:, n, P:DK]])
                project_parts(("ret", h, 2), ("ret", h, 2))
                for layer, c in ADA_AT.get(h, ()):
                    ada(layer, (c,))
                o = open_bank(("scores", h))
                for n in range(3):
                    wait_read(pe, ("qkT", h, n))
                    m = P if n < 2 else 32
                    for j in range(2):
                        last = pe.matmul(o[:, n * P:n * P + m], qkT[:, n, 2 + j, :], qkT[:, n, j, 0:m],
                                         start=j == 0, stop=j == 1, skip_group_check=True)
                sealed(last, ("scores", h))
                for n in range(3):
                    wait_read(pe, ("row", "ret", h, 1, n))
                for j in range(2):
                    o = open_bank(("S1", h, j))
                    sealed(pe.matmul(o[:, :], kd[:, 0, j * P:(j + 1) * P], v[:, 0, :], start=True, stop=True),
                           ("S1", h, j))
                o = open_bank(("part", "o", h))
                pe.wait_ge(sT_ready, h + 1)
                pe.matmul(o[0:32, :], L0["sTs"], v[:, 2, :], start=True, stop=False)
                for s in range(NS):
                    wait_unit(pe, ("state", h, s // 4))
                    old = state_slot(h, s)
                    for j in range(2):
                        n = 2 * s + j
                        g = 32 * (n % 4)
                        last = pe.matmul(o[g:g + 32, :], L0["qpad"][:, j, 32 * s:32 * s + 32], old[:, j, :],
                                         start=0 < n < 4, stop=n >= 12)
                sealed(last, ("part", "o", h))
                o = open_bank(("row", "o", h, 0))
                sealed(pe.matmul(o[:, :], L0["sT"][:, 0, :], v[:, 0, :], start=True, stop=True), ("row", "o", h, 0))
                o = open_bank(("row", "o", h, 1))
                pe.matmul(o[:, :], L0["sT"][:, 1, :], v[:, 1, :], start=True, stop=False)
                for j in range(2):
                    wait_read(pe, ("S1", h, j))
                    last = pe.matmul(o[:, :], qkT[:, 1, j, :], L0["S1"][:, j, :], start=False, stop=j == 1)
                sealed(last, ("row", "o", h, 1))
                add_groups(("o", h))
                for j in range(2):
                    o = open_bank(("S2", h, j))
                    sealed(pe.matmul(o[:, :], kd[:, 1, j * P:(j + 1) * P], v[:, 1, :], start=True, stop=True),
                           ("S2", h, j))
            def last_head_turned():
                turn_y(RH - 1)
                for n in range(3):
                    wait_read(pe, ("yT", RH - 1, n))

            assert (RH - 1) * DV >= D and 2 * NS == 2 * KT
            project(("rout", 0), L0["yT"], [("rout", 0, 0), ("rout", 0, 1)],
                    lambda i: new(RH - 1, i // 2, i % 2), last_head_turned)
            ada(1, ADA_FIRST[:3])
            project(("rout", 1), L0["yT"], [("rout", 1, 0), ("rout", 1, 1)])

            ada(1, ADA_FIRST[3:] + ADA_GATE)
            turn_h(1)

            def turn_rows(k):
                which = c - 4
                i = k - (3, 5)[which]
                if 0 <= i < 4:
                    pe.wait_ge(qk_rows, 6 * (which + 1))
                    turn(("pT", which, i // 2, i % 2),
                         [row_qk[:, which, i // 2, (4 * (i % 2) + j) * P:(4 * (i % 2) + j + 1) * P] for j in range(4)])

            for c in range(6):
                project_parts(("moba", c), ("moba", c, 0), turn_rows if c >= 4 else None)
            for which in range(2):
                for n in range(2):
                    for half in range(2):
                        wait_read(pe, ("pT", which, n, half))
            for c in (4, 5):
                for n in range(3):
                    wait_read(pe, ("row", "moba", c, n))
            kt = L1["kt"].rearrange("p (h j) n -> p h j n", h=MH)
            pts = L1["PTs"].rearrange("p w (g i m) -> p w g i m", g=4, i=4)

            def sample_scores(s):
                o = open_bank(("QK", s))
                pe.wait_ge(new_k_ready, 1)
                pe.wait_ge(kt_ready, 8 * s + 8)
                pe.wait_ge(qd_ready, s + 1)
                qs = L1["qd"][:, s % 2, :].rearrange("p (g j e m) -> p g j e m", g=4, j=4, e=2)
                for e in range(2):
                    for j in range(4):
                        for g in range(4):
                            last = pe.matmul(o[32 * g:32 * g + 32, 0:288], qs[:, g, j, e, :], kt[:, 2 * g + e, j, :],
                                             start=e == 0 and j == 0, stop=e == 1 and j == 3)
                sealed(last, ("QK", s))

            def sample_values(s):
                pe.wait_ge(P_ready, s + 1)
                o = open_bank(("PT", s))
                for j in range(2):
                    pe.transpose(o[:, j * P:(j + 1) * P], L1["x"][:, j * P:(j + 1) * P], ident)
                pe.transpose(o[0:32, 2 * P:3 * P], L1["x"][:, 2 * P:2 * P + 32], ident)
                sealed(pe.matmul(o[:, 3 * P:3 * P + 5], const("pick_den"), st(SUMS, 5), start=True, stop=True,
                                 skip_group_check=True), ("PT", s))
                o = open_bank(("PV", s))
                wait_read(pe, ("PT", s))
                for half in range(2):
                    vv = wait_unit(pe, ("v", s, half)).rearrange("p (i n) -> p i n", i=4)
                    for i in range(4):
                        for g in range(4):
                            last = pe.matmul(o[32 * g:32 * g + 8, 0:2 * DH], pts[:, half, g, i, :],
                                             vv[:, i, 2 * g * DH:2 * (g + 1) * DH], start=half == 0 and i == 0,
                                             stop=False)
                    if half == 0:
                        last.then_inc(v_half_used, 1)
                for g in range(4):
                    last = pe.matmul(o[32 * g:32 * g + 8, 0:2 * DH], pts[:, 2, g, 0, :],
                                     L1["v"][:, 2, 2 * g * DH:2 * (g + 1) * DH], start=False, stop=True)
                sealed(last, ("PV", s))

            def prompt_scores(h):
                o = open_bank(("pS", h))
                pe.matmul(o[:, 0:P], pqT[:, h, 0:P], pkT[:, h, 0:P], start=True, stop=True, skip_group_check=True)
                sealed(pe.matmul(o[:, P:3 * P], pqT[:, h, P:NP], pkT[:, h, :], start=True, stop=True,
                                 skip_group_check=True), ("pS", h))

            def prompt_values(h):
                pe.wait_ge(pP_ready, h + 1)
                turn(("pP", h), [L1["px"][:, j * P:(j + 1) * P] for j in range(3)])
                o = open_bank(("pO", h))
                wait_read(pe, ("pP", h))
                vh = [L1["v"][:, n, h * DH:(h + 1) * DH] for n in range(2)]
                pe.matmul(o[:, 0:DH], L1["pPT"][:, 0, :], vh[0], start=True, stop=True, skip_group_check=True)
                pe.matmul(o[:, DH:2 * DH], L1["pPT"][:, 1, :], vh[0], start=True, stop=False, skip_group_check=True)
                sealed(pe.matmul(o[:, DH:2 * DH], L1["pPT"][:, 2, :], vh[1], start=False, stop=True,
                                 skip_group_check=True), ("pO", h))

            def weights(tag):
                if tag == ("mout", 1):
                    pe.wait_ge(w_last_in, 16)
                    return w_last
                return wait_unit(pe, tag + (0,)).rearrange("p (k n) -> p k n", k=KT)

            def prompt_tile(tag, xT, n):
                w = weights(tag)
                o = open_bank(("row",) + tag + (n,))
                for k in range(KT):
                    last = pe.matmul(o[:, :], xT[:, k, n * P:(n + 1) * P], w[:, k, :], start=k == 0, stop=k == KT - 1)
                sealed(last, ("row",) + tag + (n,))

            def sample_tile(tag):
                w = weights(tag)
                o = open_bank(("part",) + tag)
                for k in range(KT):
                    g = 32 * (k % 4)
                    last = pe.matmul(o[g:g + 32, :], hT[:, k, NP:ROWS], w[:, k, :], start=k < 4, stop=k >= 4)
                sealed(last, ("part",) + tag)

            def head_turned(h):
                pe.wait_ge(py_ready, 2 * h + 2)
                turn(("pY", h), [py[h % 2][:, n, :] for n in range(2)])

            def sequence_turned(s):
                wait_read(pe, ("PV", s))
                turn(("OT", s), [L1["oc"]])

            def g_chunk(c, tiles):
                for n in tiles:
                    if n == 0:
                        sample_tile(("moba", c))
                    pe.wait_ge(h_joined, n + 1)
                    prompt_tile(("moba", c), hT, n)
                    if n == 1:
                        add_groups(("moba", c))

            prompt_scores(0)
            g_chunk(6, (0,))
            prompt_values(0)
            for s in range(NS):
                if s + 1 < MH:
                    prompt_scores(s + 1)
                if s == NS - 1:
                    for h in (s - 1, s):
                        head_turned(h)
                    for h in (s - 1, s):
                        wait_read(pe, ("pY", h))
                sample_scores(s)
                if s == NS - 1:
                    prompt_tile(("mout", 0), pyT, 0)
                if s == 0:
                    g_chunk(6, (1,))
                if s:
                    sequence_turned(s - 1)
                if s + 1 < MH:
                    prompt_values(s + 1)
                if 0 < s < NS - 1:
                    head_turned(s - 1)
                sample_values(s)
                if s == G_AFTER:
                    g_chunk(7, range(2))
                    for half in range(2):
                        wait_read(pe, ("row", "moba", 6 + half, 2))
                        turn(("GT", half), [L1["G"][:, 2, (4 * half + j) * P:(4 * half + j + 1) * P]
                                            for j in range(4)])
            prompt_tile(("mout", 0), pyT, 1)
            sequence_turned(NS - 1)
            prompt_tile(("mout", 1), pyT, 0)
            pe.wait_ge(yTs_ready, 1)
            sample_tile(("mout", 0))
            prompt_tile(("mout", 1), pyT, 1)
            add_groups(("mout", 0))
            sample_tile(("mout", 1))
            add_groups(("mout", 1))

        @block.scalar
        def _(act):
            readers = []

            def copy_part(tag):
                o = wait_full(act, ("part",) + tag)
                if readers:
                    wait_full(act, readers[-1])
                read_out(nc.scalar.activation(part[:, :], o[:, :], ACT.Copy), ("part",) + tag)
                readers.append(("mod", tag[1], tag[2], 1) if tag[0] == "ada" else ("row",) + tag + (2,))

            def norm_rows(layer):
                for n in range(3):
                    if layer:
                        act.wait_ge(x_done, n + 1)
                    elif n == 0:
                        act.wait_ge(x_in, 80)
                    nc.scalar.activation(h_rows[:, n, :], X[:, n, :], ACT.Square,
                                         accum_out=st(SUMSQ + n)).then_inc(sumsq, 1)
                act.wait_ge(sumsq, 3 * layer + 3)
                nc.scalar.activation(st(ROOT, 3), st(SUMSQ, 3), ACT.Sqrt, bias=const("eps"),
                                     scale=1.0 / D).then_inc(root, 1)

            def turned(dst, label, n):
                o = wait_full(act, label)
                m = P if n < 2 else 32
                read_out(nc.scalar.activation(dst[:, :, n * P:n * P + m],
                                              o[:, :].rearrange("p (k m) -> p k m", k=4)[:, :, 0:m], ACT.Copy), label)

            def high_weights(u, pairs):
                n, _ = split_at(u)
                w = wait_unit(act, u)
                for i in pairs:
                    if n:
                        if i < 3:
                            act.wait_ge(high_used, 3 * (n - 1) + i + 1)
                        else:
                            p = SPLIT[n - 1]
                            wait_full(act, ("row",) + (p if p[0] == "ret" else p[:2]) + (1,))
                    nc.scalar.activation(w_high[u[0] == "moba"][:, 2 * i:2 * i + 2, :].rearrange("p a b -> p (a b)"),
                                         w[:, 2 * i * CH:(2 * i + 2) * CH], ACT.Copy).then_inc(high_ready, 1)

            def turn_h(layer):
                for n in range(3):
                    for half in range(2):
                        if n == 2:
                            turned(hT[:, 4 * half:4 * half + 4, :], ("hT", layer, n, half), n)
                            continue
                        o = wait_full(act, ("hT", layer, n, half))
                        nc.scalar.activation(h_high[:, 4 * half:4 * half + 4, n * P:(n + 1) * P],
                                             o[:, :].rearrange("p (k m) -> p k m", k=4),
                                             ACT.Copy).then_inc(h_high_ready, 1)

            act.wait_ge(consts_in, 16)
            act.wait_ge(c_in, 32)
            nc.scalar.activation(c_rows, c_rows, ACT.Silu).then_inc(c_silu, 1)
            for c in ADA_FIRST:
                copy_part(("ada", 0, c))
                if c == ADA_FIRST[2]:
                    norm_rows(0)
            turn_h(0)
            act.wait_ge(h_ready, 3)
            high_weights(("ret", 0, 0), range(4))

            act.wait_ge(tables_in, 16)
            q, k, kd = L0["q"], L0["k"], L0["kd"]
            for h in range(RH):
                high_weights(("ret", h, 1), range(2))
                copy_part(("ret", h, 0))
                high_weights(("ret", h, 1), range(2, 4))
                if h:
                    wait_full(act, ("S2", h - 1, 1))
                    act.wait_ge(kM_ready, h)
                for n in range(3):
                    label = ("row", "ret", h, 0, n)
                    o = wait_full(act, label)
                    nc.scalar.activation(q[:, n, :], o[:, 0:DK], ACT.Copy,
                                         scale=const("qdec_p" if n < 2 else "qdec_s")[:, h:h + 1])
                    if n < 2:
                        nc.scalar.activation(kd[:, n, :], o[:, DK:2 * DK], ACT.Copy,
                                             scale=const("kdec_p")[:, h:h + 1])
                    else:
                        nc.scalar.activation(L0["kx"], o[:, DK:2 * DK], ACT.Copy, scale=const("kdec_s")[:, h:h + 1])
                        nc.scalar.activation(kmix[:, :], o[:, DK:2 * DK], ACT.Copy, scale=const("kdec_s")[:, h:h + 1])
                    read_out(nc.scalar.activation(k[:, n, :], o[:, DK:2 * DK], ACT.Copy, scale=DK ** -0.5), label)
                high_weights(("ret", h, 2), range(2))
                copy_part(("ret", h, 1))
                high_weights(("ret", h, 2), range(2, 4))
                if h:
                    for n in range(3):
                        turned(L0["yT"][:, 4 * h - 4:4 * h, :], ("yT", h - 1, n), n)
                copy_part(("ret", h, 2))
                for n in range(3):
                    label = ("row", "ret", h, 2, n)
                    o = wait_full(act, label)
                    if h:
                        act.wait_ge(y_ready, 3 * (h - 1) + n + 1)
                    read_out(nc.scalar.activation(L0["G"][:, n, :], o[:, :], ACT.Silu), label)
                for layer, c in ADA_AT.get(h, ()):
                    copy_part(("ada", layer, c))
                if h:
                    act.wait_ge(prompt_state_out, 16 * h)
                for j in range(2):
                    o = wait_full(act, ("S1", h, j))
                    read_out(nc.scalar.activation(L0["S1"][:, j, :], o[:, :], ACT.Copy), ("S1", h, j))
                copy_part(("o", h))
                for n in range(3):
                    act.wait_ge(var_ready, 3 * h + n + 1)
                    nc.scalar.activation(st(SD + n), st(MEANVAR + 2 * n + 1), ACT.Sqrt,
                                         bias=const("eps")).then_inc(sd_ready, 1)
                    if h + 1 < RH:
                        high_weights(("ret", h + 1, 0), (n,) if n < 2 else (2, 3))
            for n in range(3):
                turned(L0["yT"][:, 4 * RH - 4:4 * RH, :], ("yT", RH - 1, n), n)
            copy_part(("rout", 0))
            for c in ADA_FIRST[:3]:
                copy_part(("ada", 1, c))
            copy_part(("rout", 1))
            norm_rows(1)
            copy_part(("ada", 1, ADA_FIRST[3]))
            copy_part(("ada", 1, ADA_GATE[0]))
            act.wait_ge(prompt_state_out, 16 * RH)
            high_weights(("moba", 0, 0), range(2))
            copy_part(("ada", 1, ADA_GATE[1]))
            turn_h(1)
            high_weights(("moba", 0, 0), range(2, 4))

            for c in range(6):
                def turned_rows():
                    for n in range(2):
                        for half in range(2):
                            dst = (pqT, pkT)[c - 4]
                            turned(dst[:, 4 * half:4 * half + 4, :], ("pT", c - 4, n, half), n)

                if c < 4:
                    high_weights(("moba", c + 1, 0), range(2))
                copy_part(("moba", c))
                if c == 4:
                    turned_rows()
                    high_weights(("moba", c + 1, 0), range(2))
                if c < 5:
                    high_weights(("moba", c + 1, 0), range(2, 4))
                for n in range(3):
                    label = ("row", "moba", c, n)
                    done = 3 * c + n
                    if c < 4:
                        o = wait_full(act, label)
                        if done:
                            act.wait_ge(ms_ready, done)
                        nc.scalar.activation(squares, o[:, :], ACT.Square).then_inc(sq_ready, 1)
                        act.wait_ge(ms_ready, done + 1)
                        nc.scalar.activation(st(MSD, 4), st(MS, 4), ACT.Sqrt, bias=const("eps"),
                                             scale=1.0 / DH).then_inc(msd_ready, 1)
                if c == 5:
                    turned_rows()
                if c == 4:
                    act.wait_ge(qk_rows, 12)
                    kp = t["k_prompt"][0, 0].rearrange("(n p) h d -> n p (h d)", p=P)
                    for n in range(2):
                        act.dma_start(kp[n], row_qk[:, 1, n, :]).then_inc(k_out, 16)
                    act.dma_start(t["k_sample"][0].rearrange("b s h d -> (b s) (h d)"), row_qk[0:32, 1, 2, :]
                                  ).then_inc(k_out, 16)
            px, x = L1["px"], L1["x"]

            def prompt_exps(h):
                act.wait_ge(px_ready, h + 1)
                nc.scalar.activation(px[:, 0:P], px[:, 0:P], ACT.Exp, bias=st(PNEG), accum_out=st(PSUM))
                nc.scalar.activation(px[:, P:3 * P], px[:, P:3 * P], ACT.Exp, bias=st(PNEG + 1),
                                     accum_out=st(PSUM + 1)).then_inc(pP_ready, 1)

            def prompt_turned(h):
                o = wait_full(act, ("pP", h))
                if h:
                    wait_full(act, ("pO", h - 1))
                read_out(nc.scalar.activation(L1["pPT"].rearrange("p a b -> p (a b)"), o[:, 0:3 * P], ACT.Copy),
                         ("pP", h))

            def prompt_rows(h):
                act.wait_ge(pr_ready, h + 1)
                o = wait_full(act, ("pO", h))
                if h >= 2:
                    wait_full(act, ("pY", h - 2))
                nc.scalar.activation(py[h % 2][:, 0, :], o[:, 0:DH], ACT.Copy, scale=st(PRS))
                read_out(nc.scalar.activation(py[h % 2][:, 1, :], o[:, DH:2 * DH], ACT.Copy, scale=st(PRS + 1)),
                         ("pO", h))

            def gate_values(c, tiles):
                act.wait_ge(h_joined, 2)
                for n in tiles:
                    if n == 0:
                        copy_part(("moba", c))
                    label = ("row", "moba", c, n)
                    o = wait_full(act, label)
                    read_out(nc.scalar.activation(L1["G"][:, n, (c - 6) * CH:(c - 5) * CH], o[:, :], ACT.Silu), label)

            def head_turned(h):
                o = wait_full(act, ("pY", h))
                read_out(nc.scalar.activation(pyT[:, h, :], o[:, 0:NP], ACT.Copy), ("pY", h))

            def sequence_turned(s):
                o = wait_full(act, ("OT", s))
                read_out(nc.scalar.activation(
                    oT[:, :, TS * s:TS * s + TS].rearrange("p (g e) q -> p g e q", g=4),
                    o[:, 0:P].rearrange("p (g m) -> p g m", g=4)[:, :, 0:8].rearrange("p g (e q) -> p g e q", e=2),
                    ACT.Copy), ("OT", s))

            act.wait_ge(new_k_ready, 1)
            prompt_exps(0)
            gate_values(6, (0,))
            prompt_turned(0)
            prompt_rows(0)
            for s in range(NS):
                if s + 1 < MH:
                    prompt_exps(s + 1)
                if s == NS - 1:
                    head_turned(s - 1)
                    head_turned(s)
                if s:
                    sequence_turned(s - 1)
                if s + 1 < MH:
                    prompt_turned(s + 1)
                if 0 < s < NS - 1:
                    head_turned(s - 1)
                act.wait_ge(bias_ready, s + 1)
                for b in range(5):
                    m = slice(64 * b, min(64 * b + 64, 288))
                    last = nc.scalar.activation(x[:, m], x[:, m], ACT.Exp, bias=st(BIAS + b),
                                                accum_out=st(SUMS + b))
                last.then_inc(P_ready, 1)
                o = wait_full(act, ("PT", s))
                if s:
                    wait_read(act, ("PV", s - 1))
                nc.scalar.activation(L1["PTs"][:, 0:2, :].rearrange("p a b -> p (a b)"), o[:, 0:2 * P], ACT.Copy)
                nc.scalar.activation(st(DENS, 5), o[:, 3 * P:3 * P + 5], ACT.Copy, accum_out=st(DEN))
                read_out(nc.scalar.activation(L1["PTs"][0:32, 2, :], o[0:32, 2 * P:3 * P], ACT.Copy), ("PT", s))
                if s == 0:
                    gate_values(6, (1, 2))
                if s + 1 < MH:
                    prompt_rows(s + 1)
                if s == G_AFTER:
                    gate_values(7, range(3))
                    for half in range(2):
                        label = ("GT", half)
                        o = wait_full(act, label)
                        read_out(nc.scalar.activation(GT[:, 4 * half:4 * half + 4, :],
                                                      o[:, :].rearrange("p (k m) -> p k m", k=4)[:, :, 0:32],
                                                      ACT.Copy), label)
            sequence_turned(NS - 1)
            copy_part(("mout", 0))
            copy_part(("mout", 1))

        @block.gpsimd
        def _(pool):
            nc.gpsimd.memset(c_rows, 0.0).then_inc(pool_zeroed, 1)
            nc.gpsimd.memset(bias_ada[:, :], 0.0).then_inc(pool_zeroed, 1)
            wait_full(pool, ("mod", 0, ADA_FIRST[-1], 0))
            pool.dma_start(L0["gn"], t["ret_gn_g"].rearrange("o h v -> o (h v)").partition_broadcast(P)
                           ).then_inc(gn_in, 16)
            wait_read(pool, ("mod", 0, 3, 0))
            wait_read(pool, ("mod", 0, 3, 1))
            pool.dma_start(norm_b[:, :], t["norm_g"][1:2, :].partition_broadcast(P)).then_inc(norm_in[1], 16)
            y, G = L0["y"], L0["G"]
            low_weights(pool, nc.gpsimd.tensor_tensor, ("ret", 0, 0))
            pool.wait_ge(tables_in, 16)
            pool.wait_ge(gn_in, 16)
            for h in range(RH):
                if h:
                    wait_full(pool, ("new", h - 1, NS - 1, 1))
                else:
                    wait_full(pool, ("cT", 1))
                pool.wait_ge(k_parts, h + 1)
                nc.gpsimd.tensor_tensor(
                    kM[:, :, :], kmix[:, :].bitcast(F32).unsqueeze(1).broadcast_to([P, NS, DK]),
                    const("kmask_s").unsqueeze(2).broadcast_to([P, NS, DK]), ALU.mult).then_inc(kM_ready, 1)
                for n in range(3):
                    wait_read(pool, ("row", "ret", h, 2, n))
                    nc.gpsimd.tensor_tensor(G[:, n, :], G[:, n, :], L0["gn"][:, h * DV:(h + 1) * DV],
                                            ALU.mult).then_inc(gate_ready, 1)

                def gate_rows(n):
                    wait_read(pool, ("row", "o", h, n))
                    pool.wait_ge(gate_ready, 3 * h + n + 1)
                    nc.gpsimd.tensor_tensor(y[:, n, :], y[:, n, :], G[:, n, :], ALU.mult).then_inc(y_ready, 1)

                if h + 1 < RH:
                    low_weights(pool, nc.gpsimd.tensor_tensor, ("ret", h + 1, 0))
                for n in range(3):
                    gate_rows(n)
                wait_read(pool, ("S2", h, 1))
                pool.dma_start(t["state_prompt"][0, 0, h].rearrange("(k p) v -> p k v", p=P),
                               L0["S1"]).then_inc(prompt_state_out, 16)
            pool.wait_ge(prompt_state_out, 16 * RH)
            pool.wait_ge(x_done, 3)
            pool.dma_start(gains[:, 0, :], t["moba_q_g"].partition_broadcast(P)).then_inc(gains_in, 16)
            pool.dma_start(gains[:, 1, :], t["moba_k_g"].partition_broadcast(P)).then_inc(gains_in, 16)
            nc.gpsimd.memset(L1["PTs"][:, 2, :], 0.0).then_inc(pool_zeroed, 1)
            for n in range(3):
                wait_full(pool, ("hT", 1, n, 1))
            nc.gpsimd.memset(L1["qd"], 0.0).then_inc(pool_zeroed, 1)
            pool.wait_ge(gains_in, 32)
            low_weights(pool, nc.gpsimd.tensor_tensor, ("moba", 0, 0))
            for c in range(5):
                low_weights(pool, nc.gpsimd.tensor_tensor, ("moba", c + 1, 0))
                if c == 4:
                    break
                which = c // 2
                for n in range(3):
                    wait_read(pool, ("row", "moba", c, n))
                    r = row_qk[:, which, n, (c % 2) * CH:(c % 2 + 1) * CH].rearrange("p (h d) -> p h d", h=4)
                    nc.gpsimd.tensor_tensor(r, r, gains[:, which, :].unsqueeze(1).broadcast_to([P, 4, DH]),
                                            ALU.mult).then_inc(qk_rows, 1)
            pool.wait_ge(qb_ready, 1)
            pool.wait_ge(pool_zeroed, 4)
            qb = L1["qbT"].rearrange("p (g e j) m -> p g e j m", g=4, e=2)

            def pad_queries(s):
                if s >= 2:
                    wait_full(pool, ("QK", s - 2))
                    pool.wait_ge(py_ready, 2 * (s - 1))
                for i in range(4):
                    for e in range(2):
                        dst = L1["qd"][32 * i:32 * i + 32, s % 2, :].rearrange(
                            "p (g j e m) -> p g j e m", g=4, j=4, e=2)
                        at = 8 * i + TS * e
                        last = nc.gpsimd.tensor_copy(dst[:, :, :, e, at:at + TS],
                                                     qb[32 * i:32 * i + 32, :, e, :, TS * s:TS * s + TS])
                last.then_inc(qd_ready, 1)

            pool.wait_ge(low_ready["gpsimd"], KT * sum(e == "gpsimd" for e in LOW_BY.values()))
            pad_queries(0)
            pool.wait_ge(qd_ready, 1)
            for n in range(2):
                wait_full(pool, ("row", "moba", 5, n))
                ms = slice(n * P, (n + 1) * P)
                nc.gpsimd.tensor_tensor(hT[:, :, ms], h_high[:, :, ms].bitcast(F32), h_low[1][:, :, ms].bitcast(F32),
                                        ALU.add).then_inc(h_joined, 1)
            pool.wait_ge(h_joined, 2)
            for s in range(NS):
                if s + 1 < NS:
                    pad_queries(s + 1)
                    pool.wait_ge(qd_ready, s + 2)
                if s == 0:
                    vp = t["v_prompt"][0, 0].rearrange("(n p) h d -> n p (h d)", p=P)
                    for c in (4, 5):
                        for n in range(3):
                            wait_read(pool, ("row", "moba", c, n))
                    for n in range(2):
                        pool.dma_start(vp[n], L1["v"][:, n, :]).then_inc(rows_out, 16)
                    pool.dma_start(t["v_sample"][0].rearrange("b s h d -> (b s) (h d)"), L1["v"][0:32, 2, :]
                                   ).then_inc(rows_out, 16)
                h = s
                wait_read(pool, ("pO", h))
                for n in range(2):
                    wait_read(pool, ("row", "moba", 6 + h // 4, n))
                    nc.gpsimd.tensor_tensor(py[h % 2][:, n, :], py[h % 2][:, n, :],
                                            L1["G"][:, n, h * DH:(h + 1) * DH], ALU.mult).then_inc(py_ready, 1)
            pool.wait_ge(rows_out, 48)
            pool.wait_ge(k_out, 48)
            pool.wait_ge(prompt_state_out, 16 * RH)
            for i in range(2 * RH):
                pool.wait_ge(state_out[i], 64)

        @block.vector
        def _(dve):
            steps = [0]

            def link(ins):
                steps[0] += 1
                ins.then_inc(dve_step, 1)
                dve.wait_ge(dve_step, steps[0])

            for b in range(8):
                last = nc.vector.memset(bank[b][:, :], 0.0)
            last.then_inc(psum_zeroed, 1)

            def h_scaled(layer):
                dve.wait_ge(root, layer + 1)
                link(nc.vector.reciprocal(st(RSTD, 3), st(ROOT, 3)))
                for n in range(3):
                    last = nc.vector.scalar_tensor_tensor(h_rows[:, n, :], X[:, n, :], st(RSTD + n),
                                                          mod[:, 0, n // 2, :], ALU.mult, ALU.mult)
                link(last)

            def h_shifted(layer):
                for n in range(3):
                    nc.vector.tensor_tensor(h_rows[:, n, :], h_rows[:, n, :], mod[:, 1, n // 2, :],
                                            ALU.add).then_inc(h_ready, 1)

            def modulation(layer, chunks):
                for c in chunks:
                    at = (c % 2) * CH
                    for n in range(2):
                        label = ("mod", layer, c, n)
                        o = wait_full(dve, label)
                        if c // 2 == 1:
                            dve.wait_ge(norm_in[layer], 16)
                            ins = nc.vector.scalar_tensor_tensor(mod[:, 0, n, at:at + CH], o[:, :], 1.0,
                                                                 norm_b[:, at:at + CH], ALU.add, ALU.mult)
                        else:
                            ins = nc.vector.tensor_copy(mod[:, 1 + c // 4, n, at:at + CH], o[:, :])
                        read_out(ins, label)
                        wait_read(dve, label)

            def turn_h(layer):
                for n in range(2):
                    for half in range(2):
                        label = ("hT", layer, n, half)
                        o = wait_full(dve, label)
                        dve.wait_ge(h_high_ready, 4 * layer + 2 * n + half + 1)
                        ks = slice(4 * half, 4 * half + 4)
                        read_out(nc.vector.tensor_tensor(h_low[layer][:, ks, n * P:(n + 1) * P],
                                                         o[:, :].rearrange("p (k m) -> p k m", k=4),
                                                         h_high[:, ks, n * P:(n + 1) * P].bitcast(F32),
                                                         ALU.subtract), label)

            def add_to_x(tag, c, tiles=range(3)):
                cs = slice(c * CH, (c + 1) * CH)
                for n in tiles:
                    label = ("row",) + tag + (n,)
                    o = wait_full(dve, label)
                    tmp = h_rows[:, n, cs]
                    read_out(nc.vector.tensor_tensor(tmp, o[:, :], mod[:, 2, n // 2, cs], ALU.mult), label)
                    wait_read(dve, label)
                    ins = nc.vector.tensor_tensor(X[:, n, cs], X[:, n, cs], tmp, ALU.add)
                    if c == 1:
                        ins.then_inc(x_done, 1)

            for half in range(2):
                label = ("cT", half)
                o = wait_full(dve, label)
                read_out(nc.vector.tensor_copy(cT[:, 4 * half:4 * half + 4, :],
                                               o[:, :].rearrange("p (k m) -> p k m", k=4)[:, :, 0:32]), label)
            dve.wait_ge(consts_in, 16)
            modulation(0, ADA_FIRST[:2])
            h_scaled(0)
            modulation(0, ADA_FIRST[2:])
            h_shifted(0)
            turn_h(0)
            nc.vector.memset(L0["qpad"], 0.0)

            dve.wait_ge(tables_in, 16)
            v, qkT = L0["v"], L0["qkT"]

            def states(h, sequences):
                for s in sequences:
                    for j in range(2):
                        label = ("new", h, s, j)
                        o = wait_full(dve, label)
                        sv = state_slot(h, s)[:, j, :]
                        read_out(nc.vector.scalar_tensor_tensor(sv, sv, (1.0 - 2.0 ** (-5.0 - h)) ** TS, o[:, :],
                                                                ALU.mult, ALU.add), label)
                    wait_read(dve, ("new", h, s, 1))
                    dve.sem_inc(state_new, 1)

            for h in range(RH):
                gamma = 1.0 - 2.0 ** (-5.0 - h)
                if h:
                    states(h - 1, range(NS))
                low_weights(dve, nc.vector.tensor_tensor, ("ret", h, 1))
                for n in range(3):
                    label = ("row", "ret", h, 1, n)
                    o = wait_full(dve, label)
                    read_out(nc.vector.tensor_copy(v[:, n, :], o[:, :]), label)
                for n in range(3):
                    label = ("qkT", h, n)
                    o = wait_full(dve, label)
                    ins = nc.vector.tensor_copy(qkT[:, n, :, :].rearrange("p a b -> p (a b)"), o[:, :])
                    if n == 2:
                        for j in range(2):
                            ins = nc.vector.tensor_copy(
                                L0["qpad"][:, j, :].rearrange("p (s m) -> p s m", s=NS)[:, :, 0:TS],
                                o[:, j * P:j * P + 32].rearrange("p (s q) -> p s q", s=NS))
                    read_out(ins, label)
                low_weights(dve, nc.vector.tensor_tensor, ("ret", h, 2))
                wait_read(dve, ("row", "ret", h, 0, 2))
                nc.vector.tensor_tensor(kmix[2 * 32:P, :], L0["kx"][2 * 32:P, :], kmix[2 * 32:P, :].bitcast(F32),
                                        ALU.subtract).then_inc(k_parts, 1)
                wait_read(dve, ("row", "ret", h, 1, 2))
                link(nc.vector.tensor_copy(vmix[:, :], v[:, 2, :]))
                for at in (32, 96):
                    nc.vector.tensor_tensor(vmix[at:at + 32, :], v[at:at + 32, 2, :], vmix[at:at + 32, :].bitcast(F32),
                                            ALU.subtract).then_inc(v_parts, 1)
                for layer, c in ADA_AT.get(h, ()):
                    modulation(layer, (c,))
                o = wait_full(dve, ("scores", h))
                nc.vector.tensor_tensor(L0["sTs"], o[:, 2 * P:2 * P + 32],
                                        const("dec_s", "p (h m) -> p h m", h=RH)[:, h, :],
                                        ALU.mult).then_inc(sT_ready, 1)
                read_out(nc.vector.tensor_tensor(
                    L0["sT"], o[:, 0:2 * P].rearrange("p (n m) -> p n m", n=2),
                    const("dec_p", "p (h m) -> p h m", h=RH)[:, h:h + 1, :].broadcast_to([P, 2, P]),
                    ALU.mult), ("scores", h))

                def layer_norm(n):
                    label = ("row", "o", h, n)
                    o = wait_full(dve, label)
                    link(nc.vector.bn_stats(st(BN, 6), o[:, :]))
                    nc.vector.bn_aggr(st(MEANVAR + 2 * n, 2), st(BN, 6)).then_inc(var_ready, 1)
                    dve.wait_ge(sd_ready, 3 * h + n + 1)
                    link(nc.vector.reciprocal(st(RSD + n), st(SD + n)))
                    if h:
                        wait_full(dve, ("yT", h - 1, n))
                    read_out(nc.vector.tensor_scalar(L0["y"][:, n, :], o[:, :], st(MEANVAR + 2 * n), st(RSD + n),
                                                     ALU.subtract, ALU.mult), label)

                for n in range(3):
                    layer_norm(n)
                for j in range(2):
                    label = ("S2", h, j)
                    o = wait_full(dve, label)
                    S = L0["S1"][:, j, :]
                    read_out(nc.vector.scalar_tensor_tensor(S, S, gamma ** P, o[:, :], ALU.mult, ALU.add), label)
            states(RH - 1, range(NS))
            add_to_x(("rout", 0), 0)
            modulation(1, ADA_FIRST[:3])
            add_to_x(("rout", 1), 1)
            h_scaled(1)
            modulation(1, ADA_FIRST[3:])
            h_shifted(1)
            turn_h(1)
            modulation(1, ADA_GATE)

            dve.wait_ge(prompt_state_out, 16 * RH)
            for c in range(6):
                for n in range(3):
                    label = ("row", "moba", c, n)
                    done = 3 * c + n
                    o = wait_full(dve, label)
                    if c < 4:
                        dve.wait_ge(sq_ready, done + 1)
                        nc.vector.tensor_reduce(st(MS, 4), squares.rearrange("p (h d) -> p h d", h=4), AX_X,
                                                ALU.add).then_inc(ms_ready, 1)
                        dve.wait_ge(msd_ready, done + 1)
                        link(nc.vector.reciprocal(st(RMS4, 4), st(MSD, 4)))
                        dst = row_qk[:, c // 2, n, (c % 2) * CH:(c % 2 + 1) * CH].rearrange("p (h d) -> p h d", h=4)
                        ins = nc.vector.scalar_tensor_tensor(dst, o[:, :].rearrange("p (h d) -> p h d", h=4),
                                                             DH ** -0.5 if c < 2 else 1.0,
                                                             st(RMS4, 4).unsqueeze(2).broadcast_to([P, 4, DH]),
                                                             ALU.mult, ALU.mult)
                    else:
                        ins = nc.vector.tensor_copy(L1["v"][:, n, (c - 4) * CH:(c - 3) * CH], o[:, :])
                    read_out(ins, label)
                if c == 4:
                    dve.wait_ge(qk_rows, 12)
                    nc.vector.transpose(L1["qbT"].rearrange("p a b -> p (a b)"), row_qk[:, 0, 2, :]
                                        ).then_inc(qb_ready, 1)
                    link(nc.vector.transpose(norm_b[:, :], row_qk[:, 1, 2, :]))
                    link(nc.vector.memset(soft[:, 0:32], 0.0))

            def prompt_max(h):
                o = wait_full(dve, ("pS", h))
                if h:
                    wait_full(dve, ("pP", h - 1))
                read_out(nc.vector.scalar_tensor_tensor(px, const("dist_p"), -(2.0 ** (-8.0 * (h + 1) / MH)),
                                                        o[:, 0:3 * P], ALU.mult, ALU.add), ("pS", h))
                wait_read(dve, ("pS", h))
                nc.vector.tensor_reduce(st(PNEG), px[:, 0:P], AX_X, ALU.max, negate=True)
                nc.vector.tensor_reduce(st(PNEG + 1), px[:, P:3 * P], AX_X, ALU.max, negate=True).then_inc(px_ready, 1)

            def prompt_sums(h):
                dve.wait_ge(pP_ready, h + 1)
                if h:
                    wait_read(dve, ("pO", h - 1))
                nc.vector.reciprocal(st(PRS, 2), st(PSUM, 2)).then_inc(pr_ready, 1)

            px, x = L1["px"], L1["x"]
            wait_full(dve, ("pT", 1, 1, 1))
            wait_full(dve, ("row", "moba", 5, 1))
            dve.wait_ge(k_out, 48)
            kt = L1["kt"]
            nc.vector.tensor_copy(kt[:, :, 2 * P:2 * P + 32], kbT).then_inc(new_k_ready, 1)
            prompt_max(0)

            def output_rows(s):
                o = wait_full(dve, ("PV", s))
                wait_read(dve, ("PT", s))
                link(nc.vector.reciprocal(st(RDEN), st(DEN)))
                link(nc.vector.tensor_scalar(st(PICK, 2), const("hmask"), st(RDEN), None, ALU.mult))
                if s:
                    wait_full(dve, ("OT", s - 1))
                link(nc.vector.tensor_scalar(L1["oc"], o[:, 0:DH], st(PICK), None, ALU.mult))
                read_out(nc.vector.scalar_tensor_tensor(L1["oc"], o[:, DH:2 * DH], st(PICK + 1), L1["oc"],
                                                        ALU.mult, ALU.add), ("PV", s))

            blocks = lambda a, n: a.rearrange("p (b m) -> p b m", b=n)
            for s in range(NS):
                if s:
                    wait_full(dve, ("QK", s - 1))
                for pg in range(PAGES):
                    if pg % 4 == 0:
                        slot = wait_unit(dve, ("k", s, pg // 4))
                    page = slot[:, (pg % 4) * D:(pg % 4 + 1) * D].rearrange("p (b m) -> p b m", m=32)
                    nc.vector.transpose(kt[:, :, 32 * pg:32 * pg + 32], page).then_inc(kt_ready, 1)
                if s == 0:
                    prompt_sums(0)
                if s:
                    output_rows(s - 1)
                if s + 1 < MH:
                    prompt_max(s + 1)
                o = wait_full(dve, ("QK", s))
                if s:
                    wait_full(dve, ("PT", s - 1))
                nc.vector.tensor_reduce(soft[:, 4:8], blocks(o[:, 0:2 * P], 4), AX_X, ALU.add)
                nc.vector.tensor_tensor(x[:, 0:2 * P], o[:, 0:2 * P], const("alibi"), ALU.add)
                read_out(nc.vector.tensor_tensor(x[:, 2 * P:288], o[:, 2 * P:288],
                                                 const("alibi_new", "p (s m) -> p s m", s=NS)[:, s, :], ALU.add),
                         ("QK", s))
                wait_read(dve, ("QK", s))
                nc.vector.tensor_reduce(soft[:, 0:4], blocks(x[:, 0:2 * P], 4), AX_X, ALU.max)
                link(nc.vector.tensor_reduce(soft[:, 8:9], x[:, 2 * P:288], AX_X, ALU.max))
                link(nc.vector.transpose(soft[:, 32:64], soft[:, 0:32]))
                rows = soft[:, 32:64].rearrange("p (i m) -> p m i", i=4)
                nc.vector.tensor_reduce(st(86, 8), rows, AX_X, ALU.max)
                link(nc.vector.tensor_reduce(soft[:, 192:200], rows, AX_X, ALU.add))
                for at, src in ((64, st(86, 8)), (96, soft[:, 192:200])):
                    ins = nc.vector.tensor_copy(soft[:, at:at + 32].rearrange("p (i m) -> p i m", i=4),
                                                src.unsqueeze(1).broadcast_to([P, 4, 8]))
                link(ins)
                link(nc.vector.transpose(soft[:, 128:192], soft[:, 64:128]))
                bmax, bsum, new_max = soft[:, 128:132], soft[:, 164:168], soft[:, 136:137]
                link(nc.vector.tensor_reduce(st(LOW), bsum, AX_X, ALU.min))
                link(nc.vector.scalar_tensor_tensor(st(TIE, 4), bsum, st(LOW), const("tie"), ALU.is_equal, ALU.mult))
                link(nc.vector.tensor_reduce(st(TOPT), st(TIE, 4), AX_X, ALU.max))
                link(nc.vector.tensor_scalar(st(PEN, 4), st(TIE, 4), st(TOPT), NEG, ALU.is_equal, ALU.mult))
                link(nc.vector.tensor_tensor(st(BMAX, 4), bmax, st(PEN, 4), ALU.add))
                link(nc.vector.tensor_reduce(st(MAXB), st(BMAX, 4), AX_X, ALU.max))
                if s:
                    dve.wait_ge(P_ready, s)
                link(nc.vector.tensor_scalar(st(BIAS + 4), st(MAXB), new_max, -1.0, ALU.max, ALU.mult))
                nc.vector.tensor_scalar(st(BIAS, 4), st(PEN, 4), st(BIAS + 4), None, ALU.add).then_inc(bias_ready, 1)
                if s + 1 < MH:
                    prompt_sums(s + 1)
            add_to_x(("mout", 0), 0, (0,))
            output_rows(NS - 1)
            add_to_x(("mout", 0), 0, (1,))
            wait_read(dve, ("OT", NS - 1))
            wait_read(dve, ("GT", 1))
            nc.vector.tensor_tensor(hT[:, :, NP:ROWS], oT, GT, ALU.mult).then_inc(yTs_ready, 1)
            add_to_x(("mout", 1), 1, (0, 1))
            add_to_x(("mout", 0), 0, (2,))
            add_to_x(("mout", 1), 1, (2,))


_INS = ["x_prompt", "x_sample", "c_prompt", "c_sample", "state_ret", "cache_k", "cache_v", "page_table", "norm_g",
        "w_ada", "b_ada", "w_ret_in", "ret_gn_g", "w_ret_out", "w_moba_in", "moba_q_g", "moba_k_g", "w_moba_out"]
_OUTS = [("y_prompt", (1, NP, D)), ("y_sample", (NS, TS, D)), ("state_prompt", (1, 1, RH, DK, DV)),
         ("state_sample", (1, NS, RH, DK, DV)), ("k_prompt", (1, 1, NP, MH, DH)), ("v_prompt", (1, 1, NP, MH, DH)),
         ("k_sample", (1, NS, TS, MH, DH)), ("v_sample", (1, NS, TS, MH, DH))]


def kernel(**inputs):
    import concourse.bacc as _bacc
    from concourse.bass_utils import run_bass_kernel_spmd as _run

    nc = _bacc.Bacc("TRN2", target_bir_lowering=False, num_devices=1)
    arrays, t = {}, {}
    for name in _INS + ["consts"]:
        a = const_table() if name == "consts" else np.ascontiguousarray(inputs[name])
        arrays[f"in_{name}"] = a
        t[name] = nc.dram_tensor(f"in_{name}", a.shape, mybir.dt.from_np(a.dtype), kind="ExternalInput").ap()
    for name, shape in _OUTS:
        t[name] = nc.dram_tensor(f"out_{name}", shape, F32, kind="ExternalOutput").ap()
    build(nc, t)
    r = _run(nc, [arrays], core_ids=[0])
    return tuple(r.results[0][f"out_{name}"] for name, _ in _OUTS)
```
